# Optimizing a Trainium2 kernel written in Bass

```python
import jax, jax.numpy as jnp
from jax import lax
import numpy as np

D_MODEL = 2048
BATCH = 1
SEQ = 256
DEPTH = 1

HEAD_DIM = 128
MIX_WIDTH = D_MODEL
N_HEADS = MIX_WIDTH // HEAD_DIM
N_HEADS_MOBA = N_HEADS // 2
N_HEADS_DIL = N_HEADS - N_HEADS_MOBA
W_MOBA = N_HEADS_MOBA * HEAD_DIM
W_DIL = N_HEADS_DIL * HEAD_DIM
QKV_SPLITS = (W_MOBA, 2 * W_MOBA, 3 * W_MOBA, 3 * W_MOBA + W_DIL, 3 * W_MOBA + 2 * W_DIL)
ROT_DIM = HEAD_DIM // 4
ROPE_THETA = 500000.0
MOBA_BLOCK = 256
MOBA_TOPK = 3
MOBA_QCHUNK = 32
DIL_PAIRS = ((128, 1), (512, 4), (2048, 16))
DIL_BLOCK = 128
D_FF = 4 * D_MODEL
CONV_WIDTH = 3
RMS_EPS = 1e-6
SCALE = HEAD_DIM ** -0.5
NEG = -1e30

kernel_name = 'hymba_moba_dilated_convffn_block'

def rms_norm(x, g):
    xf = x.astype(jnp.float32)
    y = xf * lax.rsqrt(jnp.mean(xf * xf, axis=-1, keepdims=True) + RMS_EPS)
    return (y * g.astype(jnp.float32)).astype(x.dtype)

def partial_rope(t, positions):
    half = ROT_DIM // 2
    inv_freq = ROPE_THETA ** (-jnp.arange(half, dtype=jnp.float32) / half)
    ang = positions.astype(jnp.float32)[..., None] * inv_freq
    cos = jnp.cos(ang)[:, :, None, :]
    sin = jnp.sin(ang)[:, :, None, :]
    tr = t[..., :ROT_DIM].astype(jnp.float32)
    t1, t2 = tr[..., :half], tr[..., half:]
    rot = jnp.concatenate([t1 * cos - t2 * sin, t2 * cos + t1 * sin], axis=-1).astype(t.dtype)
    return jnp.concatenate([rot, t[..., ROT_DIM:]], axis=-1)

def moba_attention(q, k, v):
    B, S, H, Dh = q.shape
    nb = -(-S // MOBA_BLOCK)
    Sp = nb * MOBA_BLOCK
    k_top = min(MOBA_TOPK, nb - 1)
    pad = ((0, 0), (0, Sp - S), (0, 0), (0, 0))
    kbh = jnp.pad(k, pad).reshape(B, nb, MOBA_BLOCK, H, Dh).transpose(0, 3, 1, 2, 4)
    vbh = jnp.pad(v, pad).reshape(B, nb, MOBA_BLOCK, H, Dh).transpose(0, 3, 1, 2, 4)
    q_pos = jnp.arange(S, dtype=jnp.int32)
    q_blk = q_pos // MOBA_BLOCK
    qh = q.transpose(0, 2, 1, 3)
    own = jnp.broadcast_to(q_blk[None, None, :, None], (B, H, S, 1))
    own_valid = jnp.ones((B, H, S, 1), dtype=bool)
    if k_top > 0:
        k_mean = jnp.mean(kbh.astype(jnp.float32), axis=3)
        gate = jnp.einsum('bhsd,bhnd->bhsn', qh.astype(jnp.float32), k_mean)
        fully_past = jnp.arange(nb)[None, :] < q_blk[:, None]
        gate = jnp.where(fully_past, gate, NEG)
        _, top_idx = lax.top_k(gate, k_top)
        top_idx = top_idx.astype(jnp.int32)
        sel = jnp.concatenate([top_idx, own], axis=-1)
        valid = jnp.concatenate([top_idx < q_blk[:, None], own_valid], axis=-1)
    else:
        sel, valid = own, own_valid
    nsel = sel.shape[-1]
    C = MOBA_QCHUNK
    NC = S // C

    def to_chunks(t):
        return jnp.moveaxis(t.reshape((B, H, NC, C) + t.shape[3:]), 2, 0)

    bi = jnp.arange(B)[:, None, None, None]
    hi = jnp.arange(H)[None, :, None, None]

    def chunk(args):
        qc, selc, validc, posc = args
        kg = kbh[bi, hi, selc]
        vg = vbh[bi, hi, selc]
        s = jnp.einsum('bhcd,bhcjkd->bhcjk', qc, kg, preferred_element_type=jnp.float32) * SCALE
        key_pos = selc[..., None] * MOBA_BLOCK + jnp.arange(MOBA_BLOCK, dtype=jnp.int32)
        mask = validc[..., None] & (key_pos <= posc[None, None, :, None, None])
        s = jnp.where(mask, s, NEG).reshape(B, H, C, nsel * MOBA_BLOCK)
        p = jax.nn.softmax(s, axis=-1).reshape(B, H, C, nsel, MOBA_BLOCK)
        return jnp.einsum('bhcjk,bhcjkd->bhcd', p.astype(vg.dtype), vg,
                          preferred_element_type=jnp.float32)

    out = lax.map(chunk, (to_chunks(qh), to_chunks(sel), to_chunks(valid), q_pos.reshape(NC, C)))
    return jnp.moveaxis(out, 0, 2).reshape(B, H, S, Dh).transpose(0, 2, 1, 3)

def dilated_branch(q, k, v, window, dilation):
    B, S, H, Dh = q.shape
    n_back = window // dilation
    unit = dilation * DIL_BLOCK
    Sp = -(-S // unit) * unit
    L = Sp // dilation
    nblk = L // DIL_BLOCK

    def split(t):
        t = jnp.pad(t, ((0, 0), (0, Sp - S), (0, 0), (0, 0))).reshape(B, L, dilation, H, Dh)
        return t.transpose(0, 2, 3, 1, 4).reshape(B, dilation, H, nblk, DIL_BLOCK, Dh)

    def with_prev(t):
        prev = jnp.pad(t, ((0, 0), (0, 0), (0, 0), (1, 0), (0, 0), (0, 0)))[:, :, :, :-1]
        return jnp.concatenate([prev, t], axis=4)

    qs = split(q)
    kk = with_prev(split(k))
    vv = with_prev(split(v))
    s = jnp.einsum('brhnqd,brhnkd->brhnqk', qs, kk, preferred_element_type=jnp.float32) * SCALE
    qi = jnp.arange(DIL_BLOCK) + DIL_BLOCK
    ki = jnp.arange(2 * DIL_BLOCK)
    dist = qi[:, None] - ki[None, :]
    band = (dist >= 0) & (dist <= n_back)
    blk_ok = (jnp.arange(nblk)[:, None, None] > 0) | (ki[None, None, :] >= DIL_BLOCK)
    mask = band[None] & blk_ok
    s = jnp.where(mask, s, NEG)
    m = jnp.max(s, axis=-1, keepdims=True)
    p = jnp.exp(s - m)
    den = jnp.sum(p, axis=-1, keepdims=True)
    o = jnp.einsum('brhnqk,brhnkd->brhnqd', p.astype(vv.dtype), vv,
                   preferred_element_type=jnp.float32) / den
    lse = (m + jnp.log(den))[..., 0]
    o = o.reshape(B, dilation, H, L, Dh).transpose(0, 3, 1, 2, 4).reshape(B, Sp, H, Dh)[:, :S]
    lse = lse.reshape(B, dilation, H, L).transpose(0, 3, 1, 2).reshape(B, Sp, H)[:, :S]
    return o, lse

def dilated_mixture(q, k, v):
    outs, lses = [], []
    for window, dilation in DIL_PAIRS:
        o, lse = dilated_branch(q, k, v, window, dilation)
        outs.append(o)
        lses.append(lse)
    w = jax.nn.softmax(jnp.stack(lses, axis=0), axis=0)
    return jnp.sum(w[..., None] * jnp.stack(outs, axis=0), axis=0)

def conv_glu_ffn(h, w_gate, w_up, conv_w, conv_b, w_down):
    S = h.shape[1]
    g = h @ w_gate
    u = h @ w_up
    gp = jnp.pad(g, ((0, 0), (CONV_WIDTH - 1, 0), (0, 0)))
    g = conv_b + gp[:, 0:S] * conv_w[0]
    for j in range(1, CONV_WIDTH):
        g = g + gp[:, j:j + S] * conv_w[j]
    return (jax.nn.gelu(g, approximate=True) * u) @ w_down

def setup_inputs(seed: int = 0) -> dict:
    key = jax.random.key(seed)
    ks = jax.random.split(key, 14)
    f32 = jnp.float32

    def nrm(k, shape, scale):
        return jax.random.normal(k, shape, f32) * scale

    def gain(k, n):
        return 1.0 + 0.02 * jax.random.normal(k, (DEPTH, n), f32)

    return {
        'x': jax.random.normal(ks[0], (BATCH, SEQ, D_MODEL), f32),
        'positions': jnp.broadcast_to(jnp.arange(SEQ, dtype=jnp.int32), (BATCH, SEQ)),
        'attn_pre_g': gain(ks[1], D_MODEL),
        'w_qkv': nrm(ks[2], (DEPTH, D_MODEL, 3 * MIX_WIDTH), D_MODEL ** -0.5),
        'moba_out_g': gain(ks[3], W_MOBA),
        'dil_out_g': gain(ks[4], W_DIL),
        'w_o': nrm(ks[5], (DEPTH, MIX_WIDTH, D_MODEL), MIX_WIDTH ** -0.5),
        'attn_post_g': gain(ks[6], D_MODEL),
        'ffn_pre_g': gain(ks[7], D_MODEL),
        'w_gate': nrm(ks[8], (DEPTH, D_MODEL, D_FF), D_MODEL ** -0.5),
        'w_up': nrm(ks[9], (DEPTH, D_MODEL, D_FF), D_MODEL ** -0.5),
        'conv_w': nrm(ks[10], (DEPTH, CONV_WIDTH, D_FF), CONV_WIDTH ** -0.5),
        'conv_b': nrm(ks[11], (DEPTH, D_FF), 0.01),
        'w_down': nrm(ks[12], (DEPTH, D_FF, D_MODEL), D_FF ** -0.5),
        'ffn_post_g': gain(ks[13], D_MODEL),
    }

def reference(x, positions, attn_pre_g, w_qkv, moba_out_g, dil_out_g, w_o, attn_post_g,
              ffn_pre_g, w_gate, w_up, conv_w, conv_b, w_down, ffn_post_g):
    B, S, _ = x.shape
    for l in range(DEPTH):
        h = rms_norm(x, attn_pre_g[l])
        qkv = h @ w_qkv[l]
        qa, ka, va, qb, kb, vb = jnp.split(qkv, QKV_SPLITS, axis=-1)
        qa = partial_rope(qa.reshape(B, S, N_HEADS_MOBA, HEAD_DIM), positions)
        ka = partial_rope(ka.reshape(B, S, N_HEADS_MOBA, HEAD_DIM), positions)
        va = va.reshape(B, S, N_HEADS_MOBA, HEAD_DIM)
        qb = partial_rope(qb.reshape(B, S, N_HEADS_DIL, HEAD_DIM), positions)
        kb = partial_rope(kb.reshape(B, S, N_HEADS_DIL, HEAD_DIM), positions)
        vb = vb.reshape(B, S, N_HEADS_DIL, HEAD_DIM)
        oa = moba_attention(qa, ka, va).astype(x.dtype).reshape(B, S, W_MOBA)
        ob = dilated_mixture(qb, kb, vb).astype(x.dtype).reshape(B, S, W_DIL)
        mix = jnp.concatenate([rms_norm(oa, moba_out_g[l]), rms_norm(ob, dil_out_g[l])], axis=-1)
        x = x + rms_norm(mix @ w_o[l], attn_post_g[l])
        h = rms_norm(x, ffn_pre_g[l])
        y = conv_glu_ffn(h, w_gate[l], w_up[l], conv_w[l], conv_b[l], w_down[l])
        x = x + rms_norm(y, ffn_post_g[l])
    return x


_drawn_inputs = setup_inputs


def setup_inputs(seed=0):
    import zlib

    import numpy as np

    out = dict(_drawn_inputs(seed))
    spreads = {}
    factors = {'moba_out_g': 17.632,
     'dil_out_g': 16.813,
     'attn_post_g': 3.406,
     'ffn_pre_g': 3.417,
     'conv_b': 24.02,
     'ffn_post_g': 16.659}
    for name, (base, spread) in spreads.items():
        noise = np.random.default_rng([zlib.crc32(name.encode()), seed]).standard_normal(out[name].shape)
        drawn = base * np.exp(spread * noise) if base else spread * noise
        out[name] = __import__('jax').numpy.asarray(drawn.astype(out[name].dtype))
    for name, factor in factors.items():
        out[name] = (out[name] * factor).astype(out[name].dtype)
    return out
```

```python
from contextlib import ExitStack

import concourse.bass as bass
from concourse import mybir

ALU = mybir.AluOpType
ACT = mybir.ActivationFunctionType
AX_X = mybir.AxisListType.X
F32 = mybir.dt.float32
F32R = mybir.dt.float32r
I32 = mybir.dt.int32

P = 128
SEQ = 256
D = 2048
DFF = 4 * D
DH = 128
HEADS = D // DH
GROUP_HEADS = HEADS // 2
GROUP_W = GROUP_HEADS * DH
TT = SEQ // P
KT = D // P
FT = DFF // P
CHUNK = 512
CT = CHUNK // P
QUADS = HEADS // CT
CHUNKS_PER_GROUP = GROUP_W // CHUNK
UNIT = 1024
RING = 4
CHUNK_UNITS = KT // 2
QUAD_UNITS = 3 * CHUNK_UNITS
OUT_CHUNKS = D // CHUNK
O_START = QUADS * QUAD_UNITS
O_UNITS = OUT_CHUNKS * CHUNK_UNITS
F_START = O_START + O_UNITS
F_ITERS = DFF // CHUNK
F_UNITS = 2 * CHUNK_UNITS
D_START = F_START + F_ITERS * F_UNITS
D_UNITS = 8
D_ITERS = FT // 4
KEYS = 3 * P
SCALE = float(DH) ** -0.5
EPS = 1e-6
ROT = DH // 4
NEG = -1e30

TWO_PI_PARTS = (6.28125, 2029 / 2.0 ** 20, 3.019915981956753e-07)
ROUND_MAGIC = 12582912.0
PI = 3.1415925


def wait_from(eng, sem, value):
    if not isinstance(value, int) or value > 0:
        eng.wait_ge(sem, value)


class Chain:

    def __init__(self, eng, sem):
        self.eng, self.sem, self.base, self.n = eng, sem, 0, 0

    def link(self, ins):
        ins.then_inc(self.sem, 1)
        self.n += 1

    def settle(self):
        self.eng.wait_ge(self.sem, self.base + self.n)

    def mark(self):
        return self.n

    def enter(self, i, first, per_step):
        self.entry = self.base + self.n
        self.base = (i - first) * per_step + self.entry
        self.per_step, self.n = per_step, 0

    def leave(self, steps):
        assert self.n == self.per_step, (self.n, self.per_step)
        self.base, self.n = self.entry + steps * self.per_step, 0


def layer_kernel(nc, x, positions, attn_pre_g, w_qkv, moba_dil_g, w_o, attn_post_g, ffn_pre_g,
                 w_gate, w_up, conv, w_down, ffn_post_g, identity, score_mask, key_count,
                 rope_cols, out):
    with ExitStack() as ctx:
        def sb(name, shape, dt=F32):
            return ctx.enter_context(nc.sbuf_tensor(name, shape, dt))

        def sem(name):
            return ctx.enter_context(nc.semaphore(name))

        resid = sb("resid", [P, TT, D])
        hT_hi = sb("hT_hi", [P, KT, SEQ], F32R)
        hT_lo = sb("hT_lo", [P, KT, SEQ], F32R)
        stage = [sb(f"stage{s}", [P, UNIT]) for s in range(RING)]
        w_hi = [sb(f"w_hi{s}", [P, UNIT], F32R) for s in range(RING)]
        w_lo = [sb(f"w_lo{s}", [P, UNIT], F32R) for s in range(RING)]
        ident = sb("ident", [P, P])
        ones = sb("ones", [P, P])
        diag = sb("diag", [P, TT, P])
        post_g = sb("post_g", [P, D])
        ffn_g = sb("ffn_g", [P, D])
        cols = sb("cols", [P, 3 * KT])
        conv_c = sb("conv_c", [P, 4, FT])
        rope_c = sb("rope_c", [ROT, 2])
        wait_carrier = sb("wait_carrier", [ROT, 1])
        rope_cos = sb("rope_cos", [ROT, SEQ])
        rope_sin = sb("rope_sin", [ROT, SEQ])
        rms_bc = sb("rms_bc", [P, SEQ])
        group_bc = sb("group_bc", [P, SEQ])
        minus_half = sb("minus_half", [P, TT])
        sumsq = sb("sumsq", [P, TT])
        var = sb("var", [P, TT])
        rms_row = sb("rms_row", [P, TT])
        y_sumsq = sb("y_sumsq", [P, TT, OUT_CHUNKS])
        group_row = sb("group_row", [P, TT])
        chunk_trash = sb("chunk_trash", [P, CHUNK])

        KIB = 1024
        ARENA = 81 * KIB
        arena = sb("arena", [P, ARENA // 4])
        arena_at = nc.sbuf_base - ARENA
        plan = {"at": 0}

        def place(name, shape, dt=F32, at=None):
            if at is not None:
                plan["at"] = at
            size = 4
            for n in shape[1:]:
                size *= n
            t = nc.alloc_sbuf_tensor_at(name, shape, dt, offset=arena_at + plan["at"])
            plan["at"] += size
            assert plan["at"] <= ARENA, (name, plan["at"])
            return t

        mixT_hi = place("mixT_hi", [P, KT, SEQ], F32R, at=0)
        mixT_lo = place("mixT_lo", [P, KT, SEQ], F32R)
        oT = place("oT", [P, HEADS, SEQ])
        qT = place("qT", [P, CT, SEQ])
        kT = place("kT", [P, CT, SEQ])
        V = place("V", [P, TT, CHUNK])
        masked = place("masked", [P, KEYS])
        exps = place("exps", [P, KEYS])
        probs = place("probs", [P, KEYS])
        pT = place("pT", [P, KEYS])
        o_sq = place("o_sq", [P, SEQ])
        shuffled = [place(f"shuffled{s}", [ROT, SEQ]) for s in range(2)]
        mask_t = place("mask_t", [P, 2, KEYS])
        count_t = place("count_t", [P, 2, KEYS])
        row_max = sb("row_max", [P, TT])
        neg_max = sb("neg_max", [P, TT])
        den = sb("den", [P, TT])
        rden = sb("rden", [P, TT])
        y_gain = place("y_gain", [P, TT, D], at=48 * KIB)
        aT = place("aT", [P, FT, SEQ], at=0)
        gates = [place(f"gate{s}", [P, SEQ]) for s in range(2)]
        conv_acc = [place(f"conv_acc{s}", [P, SEQ]) for s in range(2)]
        act_g = place("act_g", [P, CT, SEQ])
        a_hi = [place(f"a_hi{s}", [P, 2, SEQ], F32R) for s in range(2)]
        a_lo = [place(f"a_lo{s}", [P, 2, SEQ], F32R) for s in range(2)]
        trash = place("trash", [P, TT, D], at=0)
        y_out = place("y_out", [P, TT, D], at=0)
        angle = place("angle", [ROT, SEQ], at=48 * KIB)
        turns = place("turns", [ROT, SEQ])
        cos_arg = place("cos_arg", [ROT, SEQ])
        pos_i = place("pos_i", [ROT, SEQ], I32)

        bank = [ctx.enter_context(nc.psum_tensor(f"bank{b}", [P, CHUNK], F32)) for b in range(8)]
        Q_BANK, K_BANK, V_BANK, S_BANK, O_BANK = 0, 2, 4, 6, 7
        GATE_BANK, UP_BANK = 0, 2
        SSQ_COL = KEYS

        s_x = [sem(f"x_loaded{h}") for h in range(2)]
        s_const = sem("consts_loaded")
        s_rope_in = sem("rope_inputs_loaded")
        s_gain = sem("gain_rows_loaded")
        s_stage = [sem(f"stage_full{s}") for s in range(RING)]
        s_hi = sem("w_hi_ready")
        s_lo = sem("w_lo_ready")
        s_used = sem("unit_used")
        s_xT = sem("resid_transposed")
        s_hT_hi = sem("hT_hi_ready")
        s_hT_lo = sem("hT_lo_ready")
        s_resid = sem("resid_updated")
        s_sumsq = sem("sumsq_ready")
        s_var = sem("var_ready")
        s_rms = sem("rms_ready")
        s_diag = sem("diag_ready")
        s_bc = sem("broadcast_done")
        s_bc_copied = sem("broadcast_copied")
        s_half = sem("minus_half_ready")
        s_ones = sem("ones_ready")
        s_angle = sem("angles_ready")
        s_sin = sem("sines_ready")
        s_table = sem("rope_tables_ready")
        s_q_out = sem("q_evacuated")
        s_k_out = sem("k_evacuated")
        s_v_out = sem("v_evacuated")
        s_shuf = sem("shuffle_done")
        s_rope = sem("rope_done")
        s_score = sem("scores_ready")
        s_max = sem("row_max_ready")
        s_exp = sem("exps_ready")
        s_prob = sem("probs_ready")
        s_pT = sem("probs_transposed")
        s_pT_out = sem("pT_evacuated")
        s_pv = sem("pv_done")
        s_o_out = sem("o_evacuated")
        s_ssq = sem("head_sumsq_done")
        s_ssq_read = sem("head_sumsq_read")
        s_mix = sem("mix_ready")
        s_mix_hi = sem("mix_hi_ready")
        s_mix_lo = sem("mix_lo_ready")
        s_y_sq = sem("y_squared")
        s_y_out = sem("y_evacuated")
        s_gate_out = sem("gate_evacuated")
        s_conv = sem("conv_ready")
        s_gelu = sem("gelu_ready")
        s_gelu_rms = sem("gelu_scaled")
        s_up_out = sem("up_evacuated")
        s_a_hi = sem("a_hi_ready")
        s_a_lo = sem("a_lo_ready")
        s_d_sq = sem("down_squared")
        s_d_out = sem("down_evacuated")
        s_res = sem("result_ready")
        s_store = sem("result_stored")
        s_dve = sem("dve_steps")
        s_pool = sem("pool_steps")

        o_units = ([(c, kp) for c in range(3) for kp in range(CHUNK_UNITS // 2)]
                   + [(c, kp) for c in range(3) for kp in range(CHUNK_UNITS // 2, CHUNK_UNITS)]
                   + [(3, kp) for kp in range(CHUNK_UNITS)])
        o_last = {c: max(m for m, (cc, _) in enumerate(o_units) if cc == c) for c in range(OUT_CHUNKS)}
        ATTEND_AT = (0, 4, 8, 12)
        ATTEND_TAIL = (0, 3, 6, 9)
        TAIL_UNITS = 12
        TAIL_END = TAIL_UNITS + RING - 1

        def q_done(i):
            return i * QUAD_UNITS + CHUNK_UNITS

        def k_done(i):
            return i * QUAD_UNITS + 2 * CHUNK_UNITS

        def v_done(i):
            return i * QUAD_UNITS + 3 * CHUNK_UNITS

        def y_done(c):
            return O_START + o_last[c] + 1

        def gate_done(i):
            return i * F_UNITS + (F_START + CHUNK_UNITS)

        def up_done(i):
            return i * F_UNITS + (F_START + F_UNITS)

        DOWN_DONE = D_START + D_ITERS * D_UNITS

        x_rows = x.rearrange("(t p) d -> p t d", p=P)
        out_rows = out.rearrange("(t p) d -> p t d", p=P)
        qkv_rows = w_qkv.rearrange("(k p) n -> p k n", p=P)
        o_rows = w_o.rearrange("(k p) n -> p k n", p=P)
        gate_rows = w_gate.rearrange("(k p) n -> p k n", p=P)
        up_rows = w_up.rearrange("(k p) n -> p k n", p=P)
        down_rows = w_down.rearrange("(k p) n -> p k n", p=P)

        block = ctx.enter_context(nc.Block())

        @block.sync
        def _(sp):
            def load(rnd, s, src, parts):
                wait_from(sp, s_lo, 4 * rnd + s - 3)
                dst = stage[s][:, :].rearrange("p (a n) -> p a n", a=parts)
                sp.dma_start(dst, src).then_inc(s_stage[s], 16)

            for h in range(2):
                for t in range(TT):
                    sp.dma_start(resid[:, t, h * (D // 2):(h + 1) * (D // 2)],
                                 x_rows[:, t, h * (D // 2):(h + 1) * (D // 2)]).then_inc(s_x[h], 16)

            def load_quad(i):
                for part in range(3):
                    col = (i // CHUNKS_PER_GROUP) * (3 * GROUP_W) + part * GROUP_W \
                        + (i % CHUNKS_PER_GROUP) * CHUNK
                    for kp in range(CHUNK_UNITS):
                        n = part * CHUNK_UNITS + kp
                        load(i * (QUAD_UNITS // RING) + n // RING, n % RING,
                             qkv_rows[:, 2 * kp:2 * kp + 2, bass.ds(col, CHUNK)], 2)

            load_quad(0)
            with sp.Fori(1, QUADS - 1) as i:
                load_quad(i)
            load_quad(QUADS - 1)
            for m, (c, kp) in enumerate(o_units):
                load((O_START + m) // RING, m % RING,
                     o_rows[:, 2 * kp:2 * kp + 2, c * CHUNK:(c + 1) * CHUNK], 2)

            with sp.Fori(0, F_ITERS) as i:
                for n in range(F_UNITS):
                    rows = gate_rows if n < CHUNK_UNITS else up_rows
                    kp = n % CHUNK_UNITS
                    load(i * (F_UNITS // RING) + F_START // RING + n // RING, n % RING,
                         rows[:, 2 * kp:2 * kp + 2, bass.ds(i * CHUNK, CHUNK)], 2)

            with sp.Fori(0, D_ITERS) as i:
                for n in range(D_UNITS):
                    load(i * (D_UNITS // RING) + D_START // RING + n // RING, n % RING,
                         down_rows[:, bass.ds(i * 4 + n // 2, 1), (n % 2) * UNIT:(n % 2 + 1) * UNIT], 1)

            for c in range(OUT_CHUNKS):
                for t in range(TT):
                    sp.wait_ge(s_res, c * TT + t + 1)
                    sp.dma_start(out_rows[:, t, c * CHUNK:(c + 1) * CHUNK],
                                 y_out[:, t, c * CHUNK:(c + 1) * CHUNK]).then_inc(s_store, 16)
            sp.wait_ge(s_store, 16 * OUT_CHUNKS * TT)

        @block.scalar
        def _(act):
            act.dma_start(pos_i[:, :], positions.to_broadcast((ROT, SEQ))).then_inc(s_rope_in, 16)
            act.dma_start(rope_c[:, :], rope_cols).then_inc(s_rope_in, 16)
            act.dma_start(ident[:, :], identity).then_inc(s_const, 16)
            act.dma_start(cols[:, 0:KT], attn_pre_g).then_inc(s_const, 16)
            act.dma_start(cols[:, KT:2 * KT], ffn_pre_g).then_inc(s_const, 16)
            act.dma_start(cols[:, 2 * KT:3 * KT], moba_dil_g).then_inc(s_const, 16)
            act.dma_start(conv_c[:, :, :], conv).then_inc(s_const, 16)
            act.dma_start(mask_t[:, :, :], score_mask.rearrange("g p k -> p g k")).then_inc(s_const, 16)
            act.dma_start(count_t[:, :, :], key_count.rearrange("g p k -> p g k")).then_inc(s_const, 16)
            act.dma_start(post_g[:, :], attn_post_g.to_broadcast((P, D))).then_inc(s_gain, 16)
            act.dma_start(ffn_g[:, :], ffn_post_g.to_broadcast((P, D))).then_inc(s_gain, 16)

            def high_part(rnd, s):
                act.wait_ge(s_stage[s], 16 * (rnd + 1))
                wait_from(act, s_used, 4 * rnd + s - 3)
                nc.scalar.copy(w_hi[s][:, :], stage[s][:, :]).then_inc(s_hi, 1)

            def residual_high(b, done, gain):
                act.wait_ge(s_xT, done + b + 1)
                for kk in range(2):
                    k = 2 * b + kk
                    nc.scalar.activation(hT_hi[:, k, :], bank[4 + b % 4][:, kk * SEQ:(kk + 1) * SEQ],
                                         ACT.Copy, scale=cols[:, gain + k:gain + k + 1]).then_inc(s_hT_hi, 1)

            def residual_sumsq():
                for t in range(TT):
                    nc.scalar.activation(trash[:, t, :], resid[:, t, :], ACT.Square,
                                         accum_out=sumsq[:, t:t + 1]).then_inc(s_sumsq, 1)

            def attend(i, n, at):
                for h in range(CT):
                    g = i * CT + (h - CT)
                    if n == at[h] + 4:
                        act.wait_ge(s_max, g + 1)
                        for t, (a, b) in enumerate(((0, P), (P, KEYS))):
                            nc.scalar.activation(exps[:, a:b], masked[:, a:b], ACT.Exp, scale=SCALE,
                                                 bias=neg_max[:, t:t + 1]).then_inc(s_exp, 1)
                    if n == at[h] + 6:
                        act.wait_ge(s_pT, g + 1)
                        nc.scalar.copy(pT[:, :], bank[O_BANK][:, 0:KEYS]).then_inc(s_pT_out, 1)
                    if n == at[h] + 7:
                        act.wait_ge(s_pv, g + 1)
                        nc.scalar.copy(oT[:, bass.ds(g, 1), :],
                                       bank[O_BANK][:, 0:SEQ]).then_inc(s_o_out, 1)
                        nc.scalar.activation(o_sq[:, :], bank[O_BANK][:, 0:SEQ],
                                             ACT.Square).then_inc(s_o_out, 1)

            def v_rows(i):
                act.wait_ge(s_used, v_done(i))
                for t in range(TT):
                    nc.scalar.activation(V[:, t, :], bank[V_BANK + t][:, :], ACT.Copy,
                                         scale=rms_row[:, t:t + 1]).then_inc(s_v_out, 1)

            def mix_high(half):
                act.wait_ge(s_mix, (half + 1) * CT)
                nc.scalar.copy(mixT_hi[:, half * CT:(half + 1) * CT, :],
                               oT[:, half * CT:(half + 1) * CT, :]).then_inc(s_mix_hi, 1)

            act.wait_ge(s_const, 16 * 7)
            act.wait_ge(s_angle, 1)
            nc.scalar.activation(rope_sin[:, :], angle[:, :], ACT.Sin).then_inc(s_sin, 1)
            nc.scalar.activation(rope_cos[:, :], cos_arg[:, :], ACT.Sin).then_inc(s_sin, 1)

            def quad(i):
                for n in range(QUAD_UNITS):
                    if isinstance(i, int) and i == 0:
                        if n < KT // 2:
                            residual_high(n, 0, 0)
                        if n == 8:
                            residual_sumsq()
                    high_part(i * (QUAD_UNITS // RING) + n // RING, n % RING)
                    if isinstance(i, int) and i == 0:
                        continue
                    if n == 3:
                        v_rows(i - 1)
                    attend(i, n, ATTEND_AT)
                    if isinstance(i, int) and n in (10, 14):
                        mix_high((n - 10) // 4)

            quad(0)
            with act.Fori(1, QUADS - 1) as i:
                quad(i)
            quad(QUADS - 1)

            def y_squares(c, t, b, signal):
                wait_from(act, signal, c * TT + t)
                nc.scalar.activation(chunk_trash[:, :], bank[b][:, :], ACT.Square,
                                     accum_out=y_sumsq[:, t, c:c + 1]).then_inc(signal, 1)

            for m in range(O_UNITS):
                high_part((O_START + m) // RING, m % RING)
                if m == 3:
                    v_rows(QUADS - 1)
                attend(QUADS, m, ATTEND_TAIL)
                if m == TAIL_END:
                    attend(QUADS, m + 1, ATTEND_TAIL)
                    mix_high(2)
                    mix_high(3)
                for c in range(OUT_CHUNKS - 1):
                    if m == min(o_last[c] + 4, O_UNITS - 1):
                        act.wait_ge(s_used, y_done(c))
                        for t in range(TT):
                            y_squares(c, t, 2 * c + t, s_y_sq)

            def high_parts_ahead(n0, n1):
                for n in range(n0, n1):
                    high_part((F_START + n) // RING, n % RING)

            high_parts_ahead(0, RING)
            c = OUT_CHUNKS - 1
            act.wait_ge(s_used, y_done(c))
            for t in range(TT):
                y_squares(c, t, 2 * c + t, s_y_sq)

            def ffn_gelu(i, n):
                j = n - 12
                if not 0 <= j < CT:
                    return
                wait_from(act, s_up_out, i * CT)
                act.wait_ge(s_conv, i * CT + j + 1)
                nc.scalar.activation(act_g[:, j, :], conv_acc[j % 2][:, :],
                                     ACT.Gelu_apprx_tanh).then_inc(s_gelu, 1)

            for n in range(F_UNITS):
                if n < KT // 2:
                    residual_high(n, KT // 2, KT)
                if n == 8:
                    act.wait_ge(s_resid, OUT_CHUNKS * TT)
                    residual_sumsq()
                if n >= RING:
                    high_part((F_START + n) // RING, n % RING)
                ffn_gelu(0, n)
            with act.Fori(1, F_ITERS) as i:
                for n in range(F_UNITS):
                    high_part(i * (F_UNITS // RING) + F_START // RING + n // RING, n % RING)
                    ffn_gelu(i, n)

            def down(i):
                for n in range(D_UNITS):
                    if n % 4 == 0:
                        kk = n // 4
                        wait_from(act, s_used, i * D_UNITS + (D_START + n - 4)
                                  if not (isinstance(i, int) and i == 0) else 0)
                        if isinstance(i, int) and i == 0:
                            act.wait_ge(s_up_out, 4)
                        nc.scalar.copy(a_hi[kk][:, :, :],
                                       aT[:, bass.ds(i * 4 + 2 * kk, 2), :]).then_inc(s_a_hi, 1)
                    high_part(i * (D_UNITS // RING) + D_START // RING + n // RING, n % RING)

            down(0)
            act.wait_ge(s_up_out, FT)
            with act.Fori(1, D_ITERS) as i:
                down(i)
            act.wait_ge(s_used, DOWN_DONE)
            for c in range(OUT_CHUNKS):
                for t in range(TT):
                    y_squares(c, t, (4 if c < 2 else 0) + 2 * (c % 2) + t, s_d_sq)

        @block.gpsimd
        def _(pool):
            chain = Chain(pool, s_pool)
            nc.gpsimd.memset(ones[:, :], 1.0).then_inc(s_ones, 1)
            nc.gpsimd.memset(minus_half[:, :], -0.5).then_inc(s_half, 1)
            pool.wait_ge(s_half, 1)

            def inverse_root(k, dst=rms_row):
                pool.wait_ge(s_var, k + 1)
                nc.gpsimd.tensor_tensor(dst[:, :], var[:, :], minus_half[:, :], ALU.pow).then_inc(s_rms, 1)

            inverse_root(0)
            pool.wait_ge(s_table, 1)

            def rotate(idx, t, h):
                sh = shuffled[h % 2]
                pool.wait_ge(s_shuf, idx + 1)
                chain.link(nc.gpsimd.tensor_tensor(t[0:ROT, h, :], t[0:ROT, h, :], rope_cos[:, :], ALU.mult))
                chain.link(nc.gpsimd.tensor_tensor(sh[:, :], sh[:, :], rope_sin[:, :], ALU.mult))
                chain.settle()
                nc.gpsimd.tensor_tensor(t[0:ROT, h, :], t[0:ROT, h, :], sh[:, :], ALU.add).then_inc(s_rope, 1)

            def rotate_quad(i):
                for part, t in enumerate((qT, kT)):
                    for h in range(CT):
                        rotate(i * (2 * CT) + part * CT + h, t, h)

            rotate_quad(0)
            with pool.Fori(1, QUADS - 1) as i:
                chain.enter(i, 1, 4 * CT)
                rotate_quad(i)
            chain.leave(QUADS - 2)
            inverse_root(1, group_row)
            rotate_quad(QUADS - 1)
            inverse_root(2, group_row)
            inverse_root(3)
            inverse_root(4)

            def scale_gelu(i, j):
                pool.wait_ge(s_gelu, i * CT + j + 1)
                nc.gpsimd.tensor_tensor(act_g[:, j, :], act_g[:, j, :], rms_bc[:, :],
                                        ALU.mult).then_inc(s_gelu_rms, 1)

            pool.wait_ge(s_bc_copied, 4)
            with pool.Fori(0, F_ITERS) as i:
                for j in range(CT):
                    scale_gelu(i, j)
            inverse_root(5)

        @block.vector
        def _(dve):
            chain = Chain(dve, s_dve)

            def low_part(rnd, s):
                dve.wait_ge(s_hi, 4 * rnd + s + 1)
                wait_from(dve, s_used, 4 * rnd + s - 3)
                nc.vector.tensor_tensor(w_lo[s][:, :], stage[s][:, :], w_hi[s][:, :].bitcast(F32),
                                        ALU.subtract).then_inc(s_lo, 1)

            def residual_low(b, done, gain):
                dve.wait_ge(s_hT_hi, done + 2 * b + 2)
                for kk in range(2):
                    k = 2 * b + kk
                    nc.vector.scalar_tensor_tensor(
                        out=hT_lo[:, k, :], in0=bank[4 + b % 4][:, kk * SEQ:(kk + 1) * SEQ],
                        scalar=cols[:, gain + k:gain + k + 1], in1=hT_hi[:, k, :].bitcast(F32),
                        op0=ALU.mult, op1=ALU.subtract).then_inc(s_hT_lo, 1)

            def mean_square(width):
                nc.vector.tensor_scalar(var[:, :], sumsq[:, :], 1.0 / width, EPS,
                                        ALU.mult, ALU.add).then_inc(s_var, 1)

            def diagonals(k, factor=rms_row):
                dve.wait_ge(s_rms, k + 1)
                for t in range(TT):
                    nc.vector.tensor_scalar(diag[:, t, :], ident[:, :], factor[:, t:t + 1], None,
                                            ALU.mult).then_inc(s_diag, 1)

            def keep_broadcast(k, dst, b):
                dve.wait_ge(s_bc, k + 1)
                nc.vector.tensor_copy(dst[:, :], bank[b][:, 0:SEQ]).then_inc(s_bc_copied, 1)

            dve.wait_ge(s_rope_in, 32)
            chain.link(nc.vector.tensor_copy(turns[:, :], pos_i[:, :]))
            chain.settle()
            chain.link(nc.vector.tensor_scalar(angle[:, :], turns[:, :], rope_c[:, 0:1], None, ALU.mult))
            chain.settle()
            chain.link(nc.vector.tensor_scalar(turns[:, :], angle[:, :], 0.15915494309189535, ROUND_MAGIC,
                                               ALU.mult, ALU.add))
            chain.settle()
            chain.link(nc.vector.tensor_scalar(turns[:, :], turns[:, :], ROUND_MAGIC, None, ALU.subtract))
            chain.settle()
            for part in TWO_PI_PARTS:
                chain.link(nc.vector.scalar_tensor_tensor(out=angle[:, :], in0=turns[:, :], scalar=-part,
                                                          in1=angle[:, :], op0=ALU.mult, op1=ALU.add))
                chain.settle()
            chain.link(nc.vector.tensor_scalar(angle[:, :], angle[:, :], PI, -PI, ALU.min, ALU.max))
            chain.settle()
            chain.link(nc.vector.scalar_tensor_tensor(out=cos_arg[:, :], in0=angle[:, :], scalar=-1.0,
                                                      in1=angle[:, :], op0=ALU.mult, op1=ALU.max))
            chain.settle()
            nc.vector.tensor_scalar(cos_arg[:, :], cos_arg[:, :], -1.0, 1.5707963267948966,
                                    ALU.mult, ALU.add).then_inc(s_angle, 1)
            dve.wait_ge(s_sin, 2)
            nc.vector.tensor_scalar(rope_sin[:, :], rope_sin[:, :], rope_c[:, 1:2], None,
                                    ALU.mult).then_inc(s_table, 1)
            dve.wait_ge(s_const, 16 * 7)

            def attend(i, n, at, group):
                for h in range(CT):
                    g = i * CT + (h - CT)
                    if n == at[h] + 4:
                        dve.wait_ge(s_score, g + 1)
                        chain.link(nc.vector.tensor_tensor(masked[:, :], bank[S_BANK][:, 0:KEYS],
                                                           mask_t[:, group, :], ALU.add))
                        chain.settle()
                        for t, (a, b) in enumerate(((0, P), (P, KEYS))):
                            chain.link(nc.vector.tensor_reduce(row_max[:, t:t + 1], masked[:, a:b], AX_X,
                                                               ALU.max))
                        chain.settle()
                        nc.vector.tensor_scalar(neg_max[:, :], row_max[:, :], -SCALE, None,
                                                ALU.mult).then_inc(s_max, 1)
                    if n == at[h] + 5:
                        dve.wait_ge(s_exp, 2 * g + 2)
                        for t, (a, b) in enumerate(((0, P), (P, KEYS))):
                            chain.link(nc.vector.tensor_tensor_reduce(
                                probs[:, a:b], exps[:, a:b],
                                count_t[:, group, a:b],
                                1.0, 0.0, ALU.mult, ALU.add, den[:, t:t + 1]))
                        chain.settle()
                        chain.link(nc.vector.reciprocal(rden[:, :], den[:, :]))
                        chain.settle()
                        for t, (a, b) in enumerate(((0, P), (P, KEYS))):
                            nc.vector.tensor_scalar(probs[:, a:b], probs[:, a:b], rden[:, t:t + 1], None,
                                                    ALU.mult).then_inc(s_prob, 1)

            def take_head(i, part, h):
                t, b, done, left = ((qT, Q_BANK, q_done, s_q_out), (kT, K_BANK, k_done, s_k_out))[part]
                dve.wait_ge(s_used, done(i))
                wait_from(dve, s_score, i * CT + (h - CT + 1)
                          if not (isinstance(i, int) and i == 0) else 0)
                nc.vector.tensor_tensor(t[:, h, :], bank[b + h // 2][:, (h % 2) * SEQ:(h % 2 + 1) * SEQ],
                                        rms_bc[:, :], ALU.mult).then_inc(left, 1)
                dve.wait_ge(left, i * CT + h + 1)
                idx = i * (2 * CT) + part * CT + h
                wait_from(dve, s_rope, idx - 1 if not (isinstance(i, int) and i == 0 and part == 0 and h < 2)
                          else 0)
                nc.vector.tensor_copy(wait_carrier[:, :], t[0:ROT, h, 0:1])
                nc.vector.stream_shuffle(shuffled[h % 2][:, :], t[0:ROT, h, :],
                                         [(c + ROT // 2) % ROT for c in range(ROT)]).then_inc(s_shuf, 1)

            Q_AT, K_AT = (11, 12, 14, 18), (19, 20, 21, 22)

            def group_stats(g):
                dve.wait_ge(s_ssq, (g + 1) * GROUP_HEADS)
                a = SSQ_COL + g * 2 * GROUP_HEADS
                chain.link(nc.vector.tensor_reduce(
                    sumsq[:, :], bank[O_BANK][:, a:a + 2 * GROUP_HEADS].rearrange("p (h t) -> p t h", t=TT),
                    AX_X, ALU.add))
                chain.settle()
                mean_square(GROUP_W)

            def mix_heads(half):
                for k in range(half * CT, (half + 1) * CT):
                    nc.vector.scalar_tensor_tensor(out=oT[:, k, :], in0=oT[:, k, :],
                                                   scalar=cols[:, 2 * KT + k:2 * KT + k + 1],
                                                   in1=group_bc[:, :], op0=ALU.mult,
                                                   op1=ALU.mult).then_inc(s_mix, 1)

            def mix_low(half):
                dve.wait_ge(s_mix_hi, half + 1)
                sl = slice(half * CT, (half + 1) * CT)
                nc.vector.tensor_tensor(mixT_lo[:, sl, :], oT[:, sl, :], mixT_hi[:, sl, :].bitcast(F32),
                                        ALU.subtract).then_inc(s_mix_lo, 1)

            def quad(i):
                first = isinstance(i, int) and i == 0
                last = isinstance(i, int) and i == QUADS - 1
                for n in range(QUAD_UNITS):
                    if first and n < KT // 2:
                        residual_low(n, 0, 0)
                    low_part(i * (QUAD_UNITS // RING) + n // RING, n % RING)
                    if first and n == 9:
                        dve.wait_ge(s_sumsq, TT)
                        mean_square(D)
                    if first and n == 10:
                        diagonals(0)
                    if first and n == 11:
                        keep_broadcast(0, rms_bc, S_BANK)
                        dve.wait_ge(s_bc_copied, 1)
                    if last and n == 0:
                        group_stats(0)
                        diagonals(1, group_row)
                    if last and n == 3:
                        keep_broadcast(1, group_bc, O_BANK)
                        dve.wait_ge(s_bc_copied, 2)
                    if last and n in (7, 10):
                        mix_heads((n - 7) // 3)
                    if last and n in (10, 14):
                        mix_low((n - 10) // 4)
                    if not first:
                        attend(i, n, ATTEND_AT, 1 if last else 0)
                    for h in range(CT):
                        if n == Q_AT[h]:
                            take_head(i, 0, h)
                        if n == K_AT[h]:
                            take_head(i, 1, h)

            quad(0)
            with dve.Fori(1, QUADS - 1) as i:
                chain.enter(i, 1, 6 * CT)
                quad(i)
            chain.leave(QUADS - 2)
            quad(QUADS - 1)

            def take_y(c, t, k):
                dve.wait_ge(s_y_sq, k + 1)
                nc.vector.tensor_tensor(y_gain[:, t, c * CHUNK:(c + 1) * CHUNK], bank[2 * c + t][:, :],
                                        post_g[:, c * CHUNK:(c + 1) * CHUNK], ALU.mult).then_inc(s_y_out, 1)

            dve.wait_ge(s_gain, 32)
            for m in range(O_UNITS):
                low_part((O_START + m) // RING, m % RING)
                attend(QUADS, m, ATTEND_TAIL, 1)
                if m == TAIL_END:
                    group_stats(1)
                    diagonals(2, group_row)
                    keep_broadcast(2, group_bc, S_BANK)
                    dve.wait_ge(s_bc_copied, 3)
                    mix_heads(2)
                    mix_heads(3)
                    mix_low(2)
                    mix_low(3)
                for c in range(OUT_CHUNKS - 1):
                    if m == min(o_last[c] + 4, O_UNITS - 1):
                        for t in range(TT):
                            take_y(c, t, c * TT + t)
            for n in range(RING):
                low_part((F_START + n) // RING, n % RING)
            c = OUT_CHUNKS - 1
            for t in range(TT):
                take_y(c, t, c * TT + t)

            chain.link(nc.vector.tensor_reduce(sumsq[:, :], y_sumsq[:, :, :], AX_X, ALU.add))
            chain.settle()
            mean_square(D)
            dve.wait_ge(s_rms, 4)
            dve.wait_ge(s_y_out, OUT_CHUNKS * TT)

            def add_y(c):
                cs = slice(c * CHUNK, (c + 1) * CHUNK)
                for t in range(TT):
                    nc.vector.scalar_tensor_tensor(out=resid[:, t, cs], in0=y_gain[:, t, cs],
                                                   scalar=rms_row[:, t:t + 1], in1=resid[:, t, cs],
                                                   op0=ALU.mult, op1=ALU.add).then_inc(s_resid, 1)

            def take_gate(i, n):
                j = n - 11
                if not 0 <= j < CT:
                    return
                f = i * CT + j
                gate, acc = gates[j % 2], conv_acc[j % 2]

                def col(w):
                    return conv_c[:, w, bass.ds(f, 1)]

                dve.wait_ge(s_used, gate_done(i))
                if j >= 2:
                    dve.wait_ge(s_gelu, f - 1)
                elif not (isinstance(i, int) and i == 0):
                    dve.wait_ge(s_gelu, i * CT + (j - 1))
                nc.vector.tensor_tensor(gate[:, :], bank[GATE_BANK + j // 2][:, (j % 2) * SEQ:(j % 2 + 1) * SEQ],
                                        rms_bc[:, :], ALU.mult).then_inc(s_gate_out, 1)
                dve.wait_ge(s_gate_out, f + 1)
                chain.link(nc.vector.tensor_scalar(acc[:, :], gate[:, :], col(2), col(3), ALU.mult, ALU.add))
                chain.settle()
                chain.link(nc.vector.scalar_tensor_tensor(out=acc[:, 1:SEQ], in0=gate[:, 0:SEQ - 1], scalar=col(1),
                                                          in1=acc[:, 1:SEQ], op0=ALU.mult, op1=ALU.add))
                chain.settle()
                nc.vector.scalar_tensor_tensor(out=acc[:, 2:SEQ], in0=gate[:, 0:SEQ - 2], scalar=col(0),
                                               in1=acc[:, 2:SEQ], op0=ALU.mult, op1=ALU.add).then_inc(s_conv, 1)

            def take_up(i, n):
                j = n - 3
                if not 0 <= j < CT:
                    return
                dve.wait_ge(s_used, up_done(i))
                dve.wait_ge(s_gelu_rms, i * CT + j + 1)
                nc.vector.tensor_tensor(aT[:, bass.ds(i * CT + j, 1), :],
                                        bank[UP_BANK + j // 2][:, (j % 2) * SEQ:(j % 2 + 1) * SEQ],
                                        act_g[:, j, :], ALU.mult).then_inc(s_up_out, 1)

            add_y(0)
            for n in range(F_UNITS):
                if n < KT // 2:
                    if n % 2 == 0 and n // 2 + 1 < OUT_CHUNKS:
                        add_y(n // 2 + 1)
                    residual_low(n, KT, KT)
                if n >= RING:
                    low_part((F_START + n) // RING, n % RING)
                if n == 9:
                    dve.wait_ge(s_sumsq, 2 * TT)
                    mean_square(D)
                if n == 10:
                    diagonals(4)
                if n == 11:
                    keep_broadcast(3, rms_bc, S_BANK)
                    dve.wait_ge(s_bc_copied, 4)
                take_gate(0, n)
            with dve.Fori(1, F_ITERS) as i:
                chain.enter(i, 1, 2 * CT)
                for n in range(F_UNITS):
                    low_part(i * (F_UNITS // RING) + F_START // RING + n // RING, n % RING)
                    take_up(i - 1, n)
                    take_gate(i, n)
            chain.leave(F_ITERS - 1)

            def down(i):
                for n in range(D_UNITS):
                    if n % 4 == 0:
                        kk = n // 4
                        dve.wait_ge(s_a_hi, i * 2 + kk + 1)
                        nc.vector.tensor_tensor(a_lo[kk][:, :, :], aT[:, bass.ds(i * 4 + 2 * kk, 2), :],
                                                a_hi[kk][:, :, :].bitcast(F32), ALU.subtract).then_inc(s_a_lo, 1)
                    low_part(i * (D_UNITS // RING) + D_START // RING + n // RING, n % RING)
                    if isinstance(i, int) and i == 0 and n == RING - 1:
                        for j in range(CT):
                            take_up(F_ITERS - 1, 3 + j)

            down(0)
            with dve.Fori(1, D_ITERS) as i:
                down(i)

            for c in range(OUT_CHUNKS):
                cs = slice(c * CHUNK, (c + 1) * CHUNK)
                for t in range(TT):
                    dve.wait_ge(s_d_sq, c * TT + t + 1)
                    nc.vector.tensor_tensor(y_out[:, t, cs], bank[(4 if c < 2 else 0) + 2 * (c % 2) + t][:, :],
                                            ffn_g[:, cs], ALU.mult).then_inc(s_d_out, 1)
            chain.link(nc.vector.tensor_reduce(sumsq[:, :], y_sumsq[:, :, :], AX_X, ALU.add))
            chain.settle()
            mean_square(D)
            dve.wait_ge(s_rms, 6)
            dve.wait_ge(s_d_out, OUT_CHUNKS * TT)
            for c in range(OUT_CHUNKS):
                cs = slice(c * CHUNK, (c + 1) * CHUNK)
                for t in range(TT):
                    nc.vector.scalar_tensor_tensor(out=y_out[:, t, cs], in0=y_out[:, t, cs],
                                                   scalar=rms_row[:, t:t + 1], in1=resid[:, t, cs],
                                                   op0=ALU.mult, op1=ALU.add).then_inc(s_res, 1)

        @block.tensor
        def _(pe):
            def transpose_residual(b, b_done):
                if b >= 4:
                    pe.wait_ge(s_hT_lo, b_done + 2 * (b - 4) + 2)
                for kk in range(2):
                    for t in range(TT):
                        k = 2 * b + kk
                        ins = nc.tensor.transpose(bank[4 + b % 4][:, kk * SEQ + t * P:kk * SEQ + (t + 1) * P],
                                                  resid[:, t, k * P:(k + 1) * P], ident[:, :])
                ins.then_inc(s_xT, 1)

            def broadcast(k, b):
                pe.wait_ge(s_diag, (k + 1) * TT)
                for t in range(TT):
                    ins = nc.tensor.matmul(bank[b][:, t * P:(t + 1) * P], ones[:, :], diag[:, t, :],
                                           start=True, stop=True)
                ins.then_inc(s_bc, 1)

            def column_unit(rnd, s, kp, first_bank):
                pe.wait_ge(s_lo, 4 * rnd + s + 1)
                for kk in range(2):
                    k = 2 * kp + kk
                    for j in range(CT):
                        o = bank[first_bank + j // 2][:, (j % 2) * SEQ:(j % 2 + 1) * SEQ]
                        w = slice(kk * CHUNK + j * P, kk * CHUNK + (j + 1) * P)
                        nc.tensor.matmul(o, w_hi[s][:, w], hT_lo[:, k, :], start=(k == 0 and j % 2 == 0),
                                         stop=False, skip_group_check=True)
                        nc.tensor.matmul(o, w_hi[s][:, w], hT_hi[:, k, :], start=False,
                                         stop=False, skip_group_check=True)
                        ins = nc.tensor.matmul(o, w_lo[s][:, w], hT_hi[:, k, :], start=False,
                                               stop=(k == KT - 1), skip_group_check=True)
                ins.then_inc(s_used, 1)

            def row_unit(rnd, s, kp, banks, hi, lo, last):
                pe.wait_ge(s_lo, 4 * rnd + s + 1)
                for kk in range(2):
                    k = 2 * kp + kk
                    w = slice(kk * CHUNK, (kk + 1) * CHUNK)
                    for t in range(TT):
                        ts = slice(t * P, (t + 1) * P)
                        o = bank[banks + t][:, :]
                        nc.tensor.matmul(o, lo[:, k, ts], w_hi[s][:, w], start=(k == 0), stop=False,
                                         skip_group_check=True)
                        nc.tensor.matmul(o, hi[:, k, ts], w_lo[s][:, w], start=False, stop=False,
                                         skip_group_check=True)
                        ins = nc.tensor.matmul(o, hi[:, k, ts], w_hi[s][:, w], start=False, stop=last and kk == 1,
                                               skip_group_check=True)
                ins.then_inc(s_used, 1)

            def attend(i, n, at):
                for h in range(CT):
                    g = i * CT + (h - CT)
                    hs = slice(h * DH, (h + 1) * DH)
                    if n == at[h] + 3:
                        pe.wait_ge(s_pT_out, g + 1)
                        pe.wait_ge(s_v_out, i * TT)
                        o = bank[O_BANK]
                        nc.tensor.matmul(o[:, 0:P], V[:, 0, hs], pT[:, 0:P], start=True, stop=True)
                        nc.tensor.matmul(o[:, P:SEQ], V[:, 0, hs], pT[:, P:SEQ], start=True, stop=False)
                        nc.tensor.matmul(o[:, P:SEQ], V[:, 1, hs], pT[:, SEQ:KEYS], start=False,
                                         stop=True).then_inc(s_pv, 1)
                    if n == at[h] + 4:
                        pe.wait_ge(s_o_out, 2 * g + 2)
                        for t in range(TT):
                            ins = nc.tensor.matmul(bank[O_BANK][:, bass.ds(g * 2 + (SSQ_COL + t), 1)],
                                                   o_sq[:, t * P:(t + 1) * P], ones[:, 0:1],
                                                   start=True, stop=True)
                        ins.then_inc(s_ssq, 1)
                for h in range(CT):
                    g = i * CT + (h - CT)
                    if n == at[h]:
                        pe.wait_ge(s_rope, i * (2 * CT) + (h - CT + 1))
                        o = bank[S_BANK]
                        nc.tensor.matmul(o[:, 0:P], qT[:, h, 0:P], kT[:, h, 0:P], start=True, stop=True)
                        nc.tensor.matmul(o[:, P:KEYS], qT[:, h, P:SEQ], kT[:, h, :], start=True,
                                         stop=True).then_inc(s_score, 1)
                    if n == at[h] + 2:
                        pe.wait_ge(s_prob, 2 * g + 2)
                        for j in range(3):
                            ins = nc.tensor.transpose(bank[O_BANK][:, j * P:(j + 1) * P],
                                                      probs[:, j * P:(j + 1) * P], ident[:, :])
                        ins.then_inc(s_pT, 1)

            pe.wait_ge(s_const, 16 * 7)
            pe.wait_ge(s_ones, 1)

            def quad(i):
                first = isinstance(i, int) and i == 0
                last = isinstance(i, int) and i == QUADS - 1
                for n in range(QUAD_UNITS):
                    rnd, s, kp = i * (QUAD_UNITS // RING) + n // RING, n % RING, n % CHUNK_UNITS
                    if first and n < KT // 2:
                        pe.wait_ge(s_hT_lo, 2 * n + 2)
                    if not first and n == 0:
                        pe.wait_ge(s_q_out, i * CT)
                    if not first and n == CHUNK_UNITS:
                        pe.wait_ge(s_k_out, i * CT)
                    if n == 2 * CHUNK_UNITS:
                        if first:
                            pe.wait_ge(s_hT_lo, KT)
                        else:
                            pe.wait_ge(s_v_out, i * TT)
                    if n < 2 * CHUNK_UNITS:
                        column_unit(rnd, s, kp, (Q_BANK, K_BANK)[n // CHUNK_UNITS])
                    else:
                        row_unit(rnd, s, kp, V_BANK, hT_hi, hT_lo, kp == CHUNK_UNITS - 1)
                    if first and n < 4:
                        transpose_residual(n + 4, 0)
                    if first and n == 9:
                        broadcast(0, S_BANK)
                    if last and n == 0:
                        broadcast(1, O_BANK)
                    if last and n == 2:
                        pe.wait_ge(s_bc_copied, 2)
                    if not first:
                        attend(i, n, ATTEND_AT)

            for b in range(4):
                if b == 0:
                    for h in range(2):
                        pe.wait_ge(s_x[h], 16 * TT)
                transpose_residual(b, 0)
            quad(0)
            with pe.Fori(1, QUADS - 1) as i:
                quad(i)
            quad(QUADS - 1)

            pe.wait_ge(s_mix_lo, 2)
            pe.wait_ge(s_q_out, QUADS * CT)
            for m, (c, kp) in enumerate(o_units):
                if m == 4:
                    pe.wait_ge(s_k_out, QUADS * CT)
                if m == 8:
                    pe.wait_ge(s_v_out, QUADS * TT)
                if m == TAIL_UNITS:
                    attend(QUADS, m, ATTEND_TAIL)
                    attend(QUADS, m + 1, ATTEND_TAIL)
                    broadcast(2, S_BANK)
                    pe.wait_ge(s_bc_copied, 3)
                    pe.wait_ge(s_mix_lo, 4)
                row_unit((O_START + m) // RING, m % RING, kp, 2 * c, mixT_hi, mixT_lo, m == o_last[c])
                if m < TAIL_UNITS:
                    attend(QUADS, m, ATTEND_TAIL)

            def transpose_updated(b):
                pe.wait_ge(s_resid, (b // 2 + 1) * TT)
                transpose_residual(b, KT)

            pe.wait_ge(s_y_out, OUT_CHUNKS * TT)
            for b in range(4):
                transpose_updated(b)

            def ffn(i):
                first = isinstance(i, int) and i == 0
                for n in range(F_UNITS):
                    if first and n < KT // 2:
                        pe.wait_ge(s_hT_lo, KT + 2 * n + 2)
                    if not first and n == 0:
                        pe.wait_ge(s_gate_out, i * CT)
                    if not first and n == CHUNK_UNITS:
                        pe.wait_ge(s_up_out, i * CT)
                    column_unit(i * (F_UNITS // RING) + F_START // RING + n // RING, n % RING,
                                n % CHUNK_UNITS, (GATE_BANK, UP_BANK)[n // CHUNK_UNITS])
                    if first and n < 4:
                        transpose_updated(n + 4)
                    if first and n == 9:
                        broadcast(3, S_BANK)

            ffn(0)
            with pe.Fori(1, F_ITERS) as i:
                ffn(i)

            def down(i):
                first = isinstance(i, int) and i == 0
                for n in range(D_UNITS):
                    kk, half = n // 4, n % 2
                    s = n % RING
                    if n % 4 == 0:
                        pe.wait_ge(s_a_lo, i * 2 + kk + 1)
                    if first and n == 1:
                        pe.wait_ge(s_up_out, FT)
                    pe.wait_ge(s_lo, i * D_UNITS + (D_START + n + 1))
                    k = (n // 2) % 2
                    for t in range(TT):
                        ts = slice(t * P, (t + 1) * P)
                        for a, w in ((a_lo, w_hi), (a_hi, w_lo), (a_hi, w_hi)):
                            for c in range(2):
                                ins = nc.tensor.matmul(
                                    bank[(4 if half == 0 else 0) + 2 * c + t][:, :], a[kk][:, k, ts],
                                    w[s][:, c * CHUNK:(c + 1) * CHUNK],
                                    start=(first and n < 2 and a is a_lo), stop=False, skip_group_check=True)
                    ins.then_inc(s_used, 1)

            down(0)
            with pe.Fori(1, D_ITERS) as i:
                down(i)


def _columns(v):
    import numpy as np
    return np.ascontiguousarray(np.asarray(v).reshape(-1, P).T)


def _shape_constants():
    import numpy as np
    q, k = np.arange(SEQ)[:, None], np.arange(SEQ)[None, :]
    d = q - k
    causal = (d >= 0).astype(np.float32)
    branches = sum(((d >= 0) & (d % dil == 0) & (d <= win)).astype(np.float32)
                   for win, dil in ((128, 1), (512, 4), (2048, 16)))
    count = np.stack([np.concatenate([c[0:P, 0:P], c[P:SEQ, :]], axis=1) for c in (causal, branches)])
    mask = np.where(count > 0, np.float32(0), np.float32(NEG)).astype(np.float32)
    half = ROT // 2
    freq = (np.float32(500000.0) ** (-np.arange(half, dtype=np.float32) / np.float32(half))).astype(np.float32)
    rope = np.stack([np.tile(freq, 2), np.repeat(np.float32([-1, 1]), half)], axis=1).astype(np.float32)
    return np.eye(P, dtype=np.float32), mask, count.astype(np.float32), rope


def kernel(x, positions, attn_pre_g, w_qkv, moba_out_g, dil_out_g, w_o, attn_post_g,
           ffn_pre_g, w_gate, w_up, conv_w, conv_b, w_down, ffn_post_g):
    import numpy as np
    import concourse.bacc as bacc
    from concourse.bass_utils import run_bass_kernel_spmd

    identity, mask, count, rope = _shape_constants()
    conv = np.concatenate([np.asarray(conv_w)[0], np.asarray(conv_b)], axis=0)
    arrays = {
        "x": np.asarray(x).reshape(SEQ, D),
        "positions": np.asarray(positions).reshape(1, SEQ),
        "attn_pre_g": _columns(attn_pre_g),
        "w_qkv": np.asarray(w_qkv)[0],
        "moba_dil_g": np.concatenate([_columns(moba_out_g), _columns(dil_out_g)], axis=1),
        "w_o": np.asarray(w_o)[0],
        "attn_post_g": np.asarray(attn_post_g),
        "ffn_pre_g": _columns(ffn_pre_g),
        "w_gate": np.asarray(w_gate)[0],
        "w_up": np.asarray(w_up)[0],
        "conv": conv.reshape(4, FT, P).transpose(2, 0, 1),
        "w_down": np.asarray(w_down)[0],
        "ffn_post_g": np.asarray(ffn_post_g),
        "identity": identity, "score_mask": mask, "key_count": count, "rope_cols": rope,
    }
    nc = bacc.Bacc("TRN2", target_bir_lowering=False, num_devices=1)
    feeds, args = {}, []
    for name, a in arrays.items():
        a = np.ascontiguousarray(a)
        feeds[f"in_{name}"] = a
        args.append(nc.dram_tensor(f"in_{name}", a.shape, mybir.dt.from_np(a.dtype), kind="ExternalInput").ap())
    args.append(nc.dram_tensor("out", (SEQ, D), F32, kind="ExternalOutput").ap())
    layer_kernel(nc, *args)
    r = run_bass_kernel_spmd(nc, [feeds], core_ids=[0])
    return r.results[0]["out"].reshape(1, SEQ, D)
```
